# Optimizing a Trainium2 kernel written in Bass

```python
import jax, jax.numpy as jnp
from jax import lax
import numpy as np

D_MODEL = 1024
BATCH = 1
SEQ = 1024
DEPTH = 1

D_MIX = D_MODEL
D_LRU = D_MIX // 2
D_SGU = D_MIX - D_LRU
LRU_HEADS = 8
LRU_HEAD_DIM = D_LRU // LRU_HEADS
CONV_WIDTH = 4
LRU_C = 8.0
SGU_HEADS = 8
SGU_HEAD_DIM = D_SGU // SGU_HEADS
CHUNK = 128
N_EXPERTS = 32
TOP_K = 4
D_EXPERT = D_MODEL
SWIGLU_ALPHA = 1.702
SWIGLU_LIMIT = 7.0
EXPERT_BLOCK = 128
EPS = 1e-6

kernel_name = 'hymba_style_rglru_sgu_moe_adaln_layer'

def rmsnorm(x, g):
    xf = x.astype(jnp.float32)
    y = xf * lax.rsqrt(jnp.mean(xf * xf, axis=-1, keepdims=True) + EPS)
    return (y * g.astype(jnp.float32)).astype(x.dtype)

def layernorm(x, g, b):
    xf = x.astype(jnp.float32)
    mu = jnp.mean(xf, axis=-1, keepdims=True)
    var = jnp.mean(jnp.square(xf - mu), axis=-1, keepdims=True)
    y = (xf - mu) * lax.rsqrt(var + EPS)
    return (y * g.astype(jnp.float32) + b.astype(jnp.float32)).astype(x.dtype)

def rg_lru_group(xa, ya, conv_w, conv_b, wr, br, wi, bi, lam):
    bsz, s, ch = xa.shape
    xc = lax.conv_general_dilated(
        xa, conv_w[:, None, :].astype(xa.dtype), window_strides=(1,),
        padding=[(CONV_WIDTH - 1, 0)], dimension_numbers=('NWC', 'WIO', 'NWC'),
        feature_group_count=ch) + conv_b.astype(xa.dtype)
    xh = xc.reshape(bsz, s, LRU_HEADS, LRU_HEAD_DIM)
    rec = jnp.einsum('bshi,hio->bsho', xh, wr.astype(xa.dtype)).reshape(bsz, s, ch)
    inp = jnp.einsum('bshi,hio->bsho', xh, wi.astype(xa.dtype)).reshape(bsz, s, ch)
    r_gate = jax.nn.sigmoid(rec.astype(jnp.float32) + br.astype(jnp.float32))
    i_gate = jax.nn.sigmoid(inp.astype(jnp.float32) + bi.astype(jnp.float32))
    log_a = -LRU_C * r_gate * jax.nn.softplus(-lam.astype(jnp.float32))
    a = jnp.exp(log_a)
    mult = jnp.sqrt(-jnp.expm1(2.0 * log_a))
    bterm = mult * i_gate * xc.astype(jnp.float32)

    def combine(left, right):
        a1, b1 = left
        a2, b2 = right
        return a1 * a2, a2 * b1 + b2

    _, h = lax.associative_scan(combine, (a, bterm), axis=1)
    return (h * ya.astype(jnp.float32)).astype(xa.dtype)

def sgu_group(u, v, ln_g, ln_b, w_s, b_s):
    bsz, s, ch = v.shape
    v = layernorm(v, ln_g, ln_b)
    vh = v.reshape(bsz, s // CHUNK, CHUNK, SGU_HEADS, SGU_HEAD_DIM)
    causal = jnp.tril(jnp.ones((CHUNK, CHUNK), dtype=bool))
    wm = jnp.where(causal[None], w_s, 0.0).astype(v.dtype)
    mixed = jnp.einsum('hts,bnshe->bnthe', wm, vh) + b_s.T.astype(v.dtype)[None, None, :, :, None]
    return u * mixed.reshape(bsz, s, ch)

def moe(h, router_w, router_b, w_gu, b_gu, w_down, b_down):
    bsz, s, d = h.shape
    n_tok = bsz * s
    hf = h.reshape(n_tok, d)
    logits = (hf @ router_w).astype(jnp.float32) + router_b.astype(jnp.float32)
    top_logit, top_e = lax.top_k(logits, TOP_K)
    gates = jax.nn.softmax(top_logit, axis=-1)
    n_assign = n_tok * TOP_K
    flat_e = top_e.reshape(n_assign).astype(jnp.int32)
    order = jnp.argsort(flat_e)
    sorted_e = flat_e[order]
    sorted_tok = (order // TOP_K).astype(jnp.int32)
    sorted_gate = gates.reshape(n_assign)[order]
    counts = jnp.bincount(flat_e, length=N_EXPERTS).astype(jnp.int32)
    padded = (counts + EXPERT_BLOCK - 1) // EXPERT_BLOCK * EXPERT_BLOCK
    pad_end = jnp.cumsum(padded)
    pad_start = pad_end - padded
    grp_start = jnp.cumsum(counts) - counts
    dest = pad_start[sorted_e] + jnp.arange(n_assign, dtype=jnp.int32) - grp_start[sorted_e]
    n_rows = n_assign + N_EXPERTS * EXPERT_BLOCK
    n_blocks = n_rows // EXPERT_BLOCK
    row_tok = jnp.full((n_rows,), n_tok, jnp.int32).at[dest].set(sorted_tok)
    row_gate = jnp.zeros((n_rows,), jnp.float32).at[dest].set(sorted_gate)
    block_start = jnp.arange(n_blocks, dtype=jnp.int32) * EXPERT_BLOCK
    block_e = jnp.minimum(jnp.searchsorted(pad_end, block_start, side='right'), N_EXPERTS - 1)
    hf_pad = jnp.concatenate([hf, jnp.zeros((1, d), hf.dtype)], axis=0)
    xs = hf_pad[row_tok].reshape(n_blocks, EXPERT_BLOCK, d)

    def expert_block(args):
        xb, e = args
        gu = xb @ w_gu[e] + b_gu[e]
        g, lin = jnp.split(gu, 2, axis=-1)
        g = jnp.minimum(g, SWIGLU_LIMIT)
        lin = jnp.clip(lin, -SWIGLU_LIMIT, SWIGLU_LIMIT)
        act = g * jax.nn.sigmoid(SWIGLU_ALPHA * g) * (lin + 1.0)
        return act @ w_down[e] + b_down[e]

    ys = lax.map(expert_block, (xs, block_e)).reshape(n_rows, d)
    ys = ys.astype(jnp.float32) * row_gate[:, None]
    out = jnp.zeros((n_tok + 1, d), jnp.float32).at[row_tok].add(ys)[:n_tok]
    return out.reshape(bsz, s, d).astype(h.dtype)

def setup_inputs(seed: int = 0) -> dict:
    key = jax.random.key(seed)
    ks = jax.random.split(key, 32)
    f32 = jnp.float32
    L = DEPTH

    def nrm(k, shape, scale):
        return jax.random.normal(k, shape, f32) * scale

    def gain(k, shape):
        return 1.0 + 0.1 * jax.random.normal(k, shape, f32)

    a0 = jax.random.uniform(ks[12], (L, D_LRU), f32, 0.9, 0.999)
    a_base = a0 ** (1.0 / LRU_C)
    lru_lambda = jnp.log(a_base) - jnp.log1p(-a_base)
    return {
        'x': nrm(ks[0], (BATCH, SEQ, D_MODEL), 1.0),
        'c': nrm(ks[1], (BATCH, D_MODEL), 1.0),
        'ada_w': nrm(ks[2], (L, D_MODEL, 6 * D_MODEL), 0.5 * D_MODEL ** -0.5),
        'ada_b': nrm(ks[3], (L, 6 * D_MODEL), 0.02),
        'norm1_g': gain(ks[4], (L, D_MODEL)),
        'w_in': nrm(ks[5], (L, D_MODEL, 2 * D_MIX), D_MODEL ** -0.5),
        'conv_w': nrm(ks[6], (L, CONV_WIDTH, D_LRU), CONV_WIDTH ** -0.5),
        'conv_b': nrm(ks[7], (L, D_LRU), 0.02),
        'lru_wr': nrm(ks[8], (L, LRU_HEADS, LRU_HEAD_DIM, LRU_HEAD_DIM), LRU_HEAD_DIM ** -0.5),
        'lru_br': nrm(ks[9], (L, D_LRU), 0.1),
        'lru_wi': nrm(ks[10], (L, LRU_HEADS, LRU_HEAD_DIM, LRU_HEAD_DIM), LRU_HEAD_DIM ** -0.5),
        'lru_bi': nrm(ks[11], (L, D_LRU), 0.1),
        'lru_lambda': lru_lambda,
        'sgu_ln_g': gain(ks[13], (L, D_SGU)),
        'sgu_ln_b': nrm(ks[14], (L, D_SGU), 0.02),
        'sgu_w': nrm(ks[15], (L, SGU_HEADS, CHUNK, CHUNK), 0.5 * CHUNK ** -0.5),
        'sgu_b': 1.0 + nrm(ks[16], (L, SGU_HEADS, CHUNK), 0.1),
        'gnorm_lru_g': gain(ks[17], (L, D_LRU)),
        'gnorm_sgu_g': gain(ks[18], (L, D_SGU)),
        'w_out': nrm(ks[19], (L, D_MIX, D_MODEL), D_MIX ** -0.5),
        'norm2_g': gain(ks[20], (L, D_MODEL)),
        'router_w': nrm(ks[21], (L, D_MODEL, N_EXPERTS), D_MODEL ** -0.5),
        'router_b': nrm(ks[22], (L, N_EXPERTS), 0.01),
        'exp_w_gu': nrm(ks[23], (L, N_EXPERTS, D_MODEL, 2 * D_EXPERT), D_MODEL ** -0.5),
        'exp_b_gu': nrm(ks[24], (L, N_EXPERTS, 2 * D_EXPERT), 0.02),
        'exp_w_down': nrm(ks[25], (L, N_EXPERTS, D_EXPERT, D_MODEL), D_EXPERT ** -0.5),
        'exp_b_down': nrm(ks[26], (L, N_EXPERTS, D_MODEL), 0.02),
        'final_g': gain(ks[27], (D_MODEL,)),
    }

def reference(x, c, ada_w, ada_b, norm1_g, w_in, conv_w, conv_b, lru_wr, lru_br, lru_wi, lru_bi,
              lru_lambda, sgu_ln_g, sgu_ln_b, sgu_w, sgu_b, gnorm_lru_g, gnorm_sgu_g, w_out,
              norm2_g, router_w, router_b, exp_w_gu, exp_b_gu, exp_w_down, exp_b_down, final_g):
    c_act = jax.nn.silu(c)
    h = x
    for l in range(DEPTH):
        mod = c_act @ ada_w[l] + ada_b[l]
        sh1, sc1, g1, sh2, sc2, g2 = jnp.split(mod[:, None, :], 6, axis=-1)
        z = rmsnorm(h, norm1_g[l]) * (1.0 + sc1) + sh1
        proj = z @ w_in[l]
        xa, ya, u, v = jnp.split(proj, [D_LRU, 2 * D_LRU, 2 * D_LRU + D_SGU], axis=-1)
        o_lru = rg_lru_group(xa, jax.nn.gelu(ya), conv_w[l], conv_b[l], lru_wr[l], lru_br[l],
                             lru_wi[l], lru_bi[l], lru_lambda[l])
        o_sgu = sgu_group(jax.nn.gelu(u), jax.nn.gelu(v), sgu_ln_g[l], sgu_ln_b[l], sgu_w[l], sgu_b[l])
        heads = jnp.concatenate([rmsnorm(o_lru, gnorm_lru_g[l]), rmsnorm(o_sgu, gnorm_sgu_g[l])], axis=-1)
        h = h + g1 * (heads @ w_out[l])
        z2 = rmsnorm(h, norm2_g[l]) * (1.0 + sc2) + sh2
        h = h + g2 * moe(z2, router_w[l], router_b[l], exp_w_gu[l], exp_b_gu[l], exp_w_down[l], exp_b_down[l])
    return rmsnorm(h, final_g)


_drawn_inputs = setup_inputs


def setup_inputs(seed=0):
    import zlib

    import numpy as np

    out = dict(_drawn_inputs(seed))
    spreads = {}
    factors = {'conv_b': 2.976,
     'lru_br': 7.272,
     'lru_bi': 4.824,
     'sgu_ln_g': 5.187,
     'sgu_ln_b': 50.203,
     'router_b': 4.954,
     'exp_b_gu': 8.0,
     'exp_b_down': 8.0,
     'sgu_b': 3.448}
    for name, (base, spread) in spreads.items():
        noise = np.random.default_rng([zlib.crc32(name.encode()), seed]).standard_normal(out[name].shape)
        drawn = base * np.exp(spread * noise) if base else spread * noise
        out[name] = __import__('jax').numpy.asarray(drawn.astype(out[name].dtype))
    for name, factor in factors.items():
        out[name] = (out[name] * factor).astype(out[name].dtype)
    return out
```

```python
from contextlib import ExitStack

import concourse.bass as bass
from concourse import mybir

F32 = mybir.dt.float32
BF16 = mybir.dt.bfloat16
I32 = mybir.dt.int32
ACT = mybir.ActivationFunctionType
ALU = mybir.AluOpType
AX = mybir.AxisListType

P = 128
D = 1024
S = 1024
KT = D // P
TT = S // P
BANK = 512
DL = 512
CT = DL // P
NE = 32
TOPK = 4
SLOTS = 256
NB = S // SLOTS
HALVES = SLOTS // P
MAX_ITEMS = NE + S * TOPK // SLOTS
WIDTHS = (96, 128, 160, 192, 224, 256)
EPS = 1e-6
ALPHA = 1.702
LIMIT = 7.0
NEG = -3.0e38
TRASH = SLOTS
SEMW = 16

PARAM_ROWS = [("c", 8), ("norm1_g", 8), ("norm2_g", 8), ("conv_b", 4), ("lru_br", 4), ("lru_bi", 4),
              ("lru_lambda", 4), ("gnorm_lru_g", 4), ("gnorm_sgu_g", 4), ("conv_w", 16), ("ada_b", 48)]
ROW = {}
_n = 0
for _name, _rows in PARAM_ROWS:
    ROW[_name] = _n
    _n += _rows
NROWS = _n
SH1, SC1, G1, SH2, SC2, G2 = (8 * i for i in range(6))

DENSE = [("ada", 0), ("ada", 1), ("ada", 2), ("ada", 3), ("win", 0), ("ada", 4), ("ada", 5), ("win", 1),
         ("ada", 6), ("ada", 7), ("win", 2), ("ada", 8), ("ada", 9), ("win", 3), ("ada", 10), ("ada", 11),
         ("wout", 0), ("wout", 1)]
DENSE_AT = {key: n for n, key in enumerate(DENSE)}
DENSE_SLOTS = 4
CHUNKS = 12
SLOT_OF_PAIR = (2, 3, 4, 0, 1, 5)


def bank_jobs():
    jobs = [("cols", 0, "dve")]
    jobs += [("mod", j, "dve") for j in range(4)]
    jobs += [("zT", (k, th), "act") for th in range(2) for k in range(KT)]
    jobs += [("xa", (m, th), "dve") for m in range(CT) for th in range(2)]
    jobs += [("mod", j, "dve") for j in (4, 5)]
    jobs += [("g1row", q, "dve") for q in range(2)]
    for ct in range(CT):
        jobs += [("ya", (ct, th), "act") for th in range(2)]
        jobs += [(g, (ct, th), "act") for g in ("rec", "inp") for th in range(2)]
        if ct >= 2:
            jobs += [("mod", 4 + ct, "dve")]
    jobs += [("wm", q, "dve") for q in range(2)]
    jobs += [("u", (m, th), "act") for m in range(CT) for th in range(2)]
    jobs += [("mod", j, "dve") for j in (8, 9)]
    jobs += [("v", t, "act") for t in range(TT)]
    jobs += [("mod", j, "dve") for j in (10, 11)]
    jobs += [("g2row", q, "dve") for q in range(2)]
    jobs += [("ssq", (0, th), "act") for th in range(2)]
    jobs += [("mix", t, "dve") for t in range(TT)]
    jobs += [("ssq", (1, th), "act") for th in range(2)]
    for th in range(2):
        jobs += [("wo", (t, dh), "dve") for t in range(4 * th, 4 * th + 4) for dh in range(2)]
    for th in range(2):
        jobs += [("z2T", (k, th), "act") for k in range(KT)]
        jobs += [("lgT", th, "act")]
    jobs += [("lg", 0, "dve"), ("bgu", 0, "dve"), ("rank", 0, "dve"), ("rank", 1, "dve"), ("items", 0, "dve")]
    jobs += [("gT", q, "dve") for q in range(2)]
    jobs += [("bd", (t, dh), "dve") for t in range(TT) for dh in range(2)]
    return jobs


JOBS = bank_jobs()
JOB = {(name, i): n for n, (name, i, _) in enumerate(JOBS)}
BANKS = 8


def drained_by(n):
    who = JOBS[n][2]
    return who, sum(j[2] == who for j in JOBS[:n + 1])


def build(nc, ins, out):
    x, c, ada_w, ada_b = ins["x"][0], ins["c"], ins["ada_w"][0], ins["ada_b"]
    w_in, w_out = ins["w_in"][0], ins["w_out"][0]
    w_gu, w_down = ins["exp_w_gu"][0], ins["exp_w_down"][0]
    out_rows = out[0]

    hs_rows = nc.dram_tensor("hs_rows", (S + TRASH, D), F32, kind="Internal").ap()
    acc_rows = nc.dram_tensor("acc_rows", (S + TRASH, D), F32, kind="Internal").ap()

    with ExitStack() as ctx:
        def sb(name, shape, dt=F32):
            return ctx.enter_context(nc.sbuf_tensor(name, shape, dt))

        def sem(name):
            return ctx.enter_context(nc.semaphore(name))

        big = sb("big", [P, 6, 4096])
        r1 = sb("r1", [P, 8192])
        r2 = sb("r2", [P, 16384])
        psum = ctx.enter_context(nc.psum_tensor("psum", [P, BANKS, BANK], F32))

        def ring(key):
            return big[:, DENSE_AT[key] % DENSE_SLOTS, :].rearrange("p (k n) -> p k n", k=8)

        lru_t = big[:, 4, :].rearrange("p (i n) -> p i n", i=4)
        s5 = big[:, 5, :]
        ln_g = s5[:, 0:512]
        ln_b = s5[:, 512:1024]
        sgu_bias = s5[:, 1024:1536].rearrange("p (h t) -> p h t", h=4)
        wmT = s5[:, 1536:2560].rearrange("p (h t) -> p h t", h=8)
        wr_bd = s5[:, 2560:3072].rearrange("p (c n) -> p c n", c=CT)
        wi_bd = s5[:, 3072:3584].rearrange("p (c n) -> p c n", c=CT)
        router_w = s5[:, 3584:3840].rearrange("p (k e) -> p k e", k=KT)

        zT = r1[:, :].rearrange("p (k n) -> p k n", k=KT)
        h_rows = r1[:, :].rearrange("p (t n) -> p t n", t=TT)

        xaT = r2[:, 0:4096].rearrange("p (c n) -> p c n", c=CT)
        v_rows = r2[:, 4096:8192].rearrange("p (t n) -> p t n", t=TT)
        yaT = r2[:, 8192:12288].rearrange("p (c n) -> p c n", c=CT)
        uT = r2[:, 12288:16384].rearrange("p (c n) -> p c n", c=CT)
        wm_raw = r2[:, 4096:5120].rearrange("p (h t) -> p h t", h=8)
        x_rows = r2[:, 8192:16384].rearrange("p (t n) -> p t n", t=TT)
        hs_tile = r2[:, 0:4096].rearrange("p (t n) -> p t n", t=4)
        z2T = r2[:, 4096:8192].rearrange("p (k n) -> p k n", k=KT)

        zg = r2[:, 0:2048].rearrange("p (h n) -> p h n", h=HALVES)
        izT = r2[:, 2048:4096].rearrange("p (k n) -> p k n", k=KT)
        actT = r2[:, 4096:6144].rearrange("p (k n) -> p k n", k=KT)
        y_rows = r2[:, 6144:8192].rearrange("p (h n) -> p h n", h=HALVES)
        glu_t = r2[:, 8192:10240].rearrange("p (i b n) -> p i b n", i=4, b=2)
        yT = r2[:, 10240:11264].rearrange("p (b d n) -> p b d n", b=2, d=2)
        lgT_sb = r2[0:NE, 12288:13312]
        onehot = r2[:, 11264:12288].bitcast(BF16).rearrange("p (t n) -> p t n", t=TT)
        rank_at = r2[:, 12288:13312].rearrange("p (b e t) -> p b e t", b=NB, e=NE)
        gate_tab = r2[:, 13312:14080].bitcast(BF16).rearrange("p (e t i) -> p e t i", e=NE, t=TT)
        bgu_col = r2[:, 14080:14592].rearrange("p (f e) -> p f e", f=16)
        bgu_raw = r2[0:NE, 8192:10240]
        bdown_raw = r2[0:NE, 10240:11264]
        gT = r2[0:NE, 11264:12288]
        rt = r2[:, 14592:16384]
        lg36 = rt[:, 0:288].rearrange("p (t e) -> p t e", t=TT)
        mr36 = rt[:, 288:576].rearrange("p (t e) -> p t e", t=TT)
        sel = rt[:, 576:832].rearrange("p (t e) -> p t e", t=TT)
        gate = rt[:, 832:1088].rearrange("p (t e) -> p t e", t=TT)
        rank = rt[:, 1088:1344].rearrange("p (t e) -> p t e", t=TT)
        top8 = rt[:, 1344:1408].rearrange("p (t i) -> p t i", t=TT)
        rsum = rt[:, 1408:1416]
        gtmp = rt[:, 1416:1672].rearrange("p (t e) -> p t e", t=TT)
        ex4 = rt[:, 1672:1704].rearrange("p (t i) -> p t i", t=TT)

        ident = sb("ident", [P, P])
        ones = sb("ones", [P, P])
        before = s5[:, 3840:3968]
        iota_s = sb("iota_s", [P, SLOTS])
        prow = r2[:, 0:P]
        cols = sb("cols", [P, NROWS])
        cact = sb("cact", [P, KT])
        mod = sb("mod", [P, 48])
        scale1 = sb("scale1", [P, KT])
        scale2 = sb("scale2", [P, KT])
        gacc = sb("gacc", [P, 2, 512])
        g1row = sb("g1row", [P, D])
        g2row = sb("g2row", [P, D])
        ssum = sb("ssum", [P, TT])
        srt = sb("srt", [P, TT])
        rstd = sb("rstd", [P, TT])
        eps = sb("eps", [P, 1])
        tiny = sb("tiny", [P, 1])
        sp = sb("sp", [P, 8, CT])
        bn6 = sb("bn6", [P, 6])
        bn2 = sb("bn2", [P, TT, 2])
        rbias = sb("rbias", [NE, 1])
        run_off = g1row[:, 0:32]
        it_f = g1row[:, 32:288].rearrange("p (i e) -> p i e", i=8)
        it_c = g1row[:, 288:304]
        pidx = sb("pidx", [P, 1])
        iota_e = sb("iota_e", [P, NE])
        items_i = g1row[0:1, 304:304 + 3 * P + NE + 1].bitcast(I32)
        tokpart = sb("tokpart", [P, TT, 3])
        slot_c = sb("slot_c", [P, 2, HALVES])
        lst = g1row[:, 724:736].rearrange("p (h i) -> p h i", h=HALVES)
        lst_t = g1row[:, 736:744].rearrange("p (i h) -> p i h", h=HALVES)
        idx_next = sb("idx_next", [P, HALVES], I32)
        idx_cur = sb("idx_cur", [P, HALVES], I32)
        gate_next = sb("gate_next", [P, HALVES])
        gate_cur = sb("gate_cur", [P, HALVES])
        cur6 = g1row[:, 780:804].bitcast(BF16).rearrange("p (t i) -> p t i", t=TT)
        bg_cur = g1row[:, 764:780]
        final_g = big[:, SLOT_OF_PAIR[0], 0:D]

        const_made = sem("const_made")
        param_in = sem("param_in")
        mixpar_in = sem("mixpar_in")
        wm_in = sem("wm_in")
        x_in = [sem(f"x_in{t}") for t in range(TT)]
        xr_in = [sem(f"xr_in{t}") for t in range(TT)]
        dense_in = [sem(f"dense_in{n}") for n in range(DENSE_SLOTS)]
        filled = sem("filled")
        act_drained = sem("act_drained")
        dve_drained = sem("dve_drained")
        dve_chain = sem("dve_chain")
        act_chain = sem("act_chain")
        pool_chain = sem("pool_chain")
        cact_made = sem("cact_made")
        rstd_made = sem("rstd_made")
        ssum_made = sem("ssum_made")
        sqrt_made = sem("sqrt_made")
        x_scaled = sem("x_scaled")
        gemv_made = sem("gemv_made")
        affine_made = sem("affine_made")
        diag_made = sem("diag_made")
        sp_exp = sem("sp_exp")
        sp_made = sem("sp_made")
        conv_made = sem("conv_made")
        decay_made = sem("decay_made")
        mult2_made = sem("mult2_made")
        mult_made = sem("mult_made")
        lru_made = sem("lru_made")
        bn_made = sem("bn_made")
        bn_root = sem("bn_root")
        v_normed = sem("v_normed")
        v_affine = sem("v_affine")
        wm_masked = sem("wm_masked")
        sgu_made = sem("sgu_made")
        squares = sem("squares")
        heads_made = sem("heads_made")
        wout_scaled = sem("wout_scaled")
        h_root = sem("h_root")
        h_rstd = sem("h_rstd")
        hs_made = sem("hs_made")
        hs_out = sem("hs_out")
        acc_out = sem("acc_out")
        bgu_in = sem("bgu_in")
        exp_made = sem("exp_made")
        top_made = sem("top_made")
        sel_made = sem("sel_made")
        item_f_made = sem("item_f_made")
        gT_made = sem("gT_made")
        acc_made = sem("acc_made")
        items_ready = sem("items_ready")
        w_arrived = [sem(f"w_arrived{q}") for q in range(CHUNKS)]
        hot_made = sem("hot_made")
        list_made = sem("list_made")
        list_read = sem("list_read")
        idx_made = sem("idx_made")
        rows_in = [sem(f"rows_in{h}") for h in range(HALVES)]
        may_start = sem("may_start")
        zt_made = sem("zt_made")
        zt_drained = sem("zt_drained")
        gu_made = sem("gu_made")
        gu_drained = sem("gu_drained")
        sig_made = sem("sig_made")
        gsig_made = sem("gsig_made")
        act_made = sem("act_made")
        dn_made = sem("dn_made")
        dn_drained = sem("dn_drained")
        yt_made = sem("yt_made")
        yt_drained = sem("yt_drained")
        fin_in = [sem(f"fin_in{t}") for t in range(TT)]
        fing_in = sem("fing_in")
        fin_sum = sem("fin_sum")
        fin_root = sem("fin_root")
        fin_rstd = sem("fin_rstd")
        fin_scaled = sem("fin_scaled")
        fin_made = sem("fin_made")
        stored = sem("stored")

        def item_value(eng, what, g, low, high):
            return eng.value_load(items_i[0:1, bass.ds(g + what * P, 1)], min_val=low, max_val=high)

        def item_count(eng):
            return eng.value_load(items_i[0:1, 3 * P + NE:3 * P + NE + 1], min_val=NE, max_val=MAX_ITEMS)

        def bank_of(n):
            return psum[:, n % BANKS, :]

        def wait_drained(eng, n):
            who, count = drained_by(n)
            eng.wait_ge(act_drained if who == "act" else dve_drained, count)

        LAST_ACT = sum(j[2] == "act" for j in JOBS)
        LAST_DVE = sum(j[2] == "dve" for j in JOBS)

        def chunk_tile(q):
            at = (q % 2) * 2048
            return big[:, SLOT_OF_PAIR[q // 2], at:at + 2048].rearrange("p (k n) -> p k n", k=8)

        def chunk_source(e, q):
            if q < 8:
                col = (q % 2) * D + (q // 2) * 256
                w = w_gu[bass.ds(e, 1), :, col:col + 256]
            else:
                w = w_down[bass.ds(e, 1), :, (q - 8) * 256:(q - 7) * 256]
            return w.rearrange("a (k p) n -> p (a k) n", p=P)

        block = ctx.enter_context(nc.Block())

        @block.sync
        def _(sp_):
            for name, rows in PARAM_ROWS:
                src = ins[name]
                pat = {2: "a (r p) -> (a r) p", 3: "a w (r p) -> (a w r) p"}[len(src.shape)]
                sp_.dma_start(prow[ROW[name]:ROW[name] + rows, :], src.rearrange(pat, p=P)).then_inc(param_in, SEMW)
            for t in range(TT):
                sp_.dma_start(x_rows[:, t, :], x[t * P:(t + 1) * P, :]).then_inc(x_in[t], SEMW)

            for n, (kind, j) in enumerate(DENSE):
                if n >= DENSE_SLOTS:
                    old, i = DENSE[n - DENSE_SLOTS]
                    if old == "ada":
                        sp_.wait_ge(gemv_made, i + 1)
                    else:
                        last = ("v", TT - 1) if i == 3 else (("xa", "ya", "u")[i], (CT - 1, 1))
                        sp_.wait_ge(filled, JOB[last] + 1)
                w = {"ada": ada_w, "win": w_in, "wout": w_out}[kind]
                sp_.dma_start(ring((kind, j)), w[:, j * 512:(j + 1) * 512].rearrange("(k p) n -> p k n", p=P)
                              ).then_inc(dense_in[n % DENSE_SLOTS], SEMW)
            sp_.wait_ge(filled, JOB[("v", TT - 1)] + 1)
            for t in range(TT):
                sp_.dma_start(h_rows[:, t, :], x[t * P:(t + 1) * P, :]).then_inc(xr_in[t], SEMW)

            for q in range(CHUNKS):
                slot = SLOT_OF_PAIR[q // 2]
                if q == 0:
                    sp_.wait_ge(gemv_made, 12)
                if q == 4:
                    sp_.wait_ge(filled, JOB[("ssq", (1, 1))] + 1)
                if q == 6:
                    sp_.wait_ge(filled, JOB[("wo", (TT - 1, 1))] + 1)
                if q == 10:
                    sp_.wait_ge(filled, JOB[("rank", 1)] + 1)
                sp_.dma_start(chunk_tile(q), chunk_source(0, q)).then_inc(w_arrived[q], SEMW)

            sp_.wait_ge(items_ready, 1)
            with sp_.Fori(1, NE) as e:
                done = sp_.value_load(items_i[0:1, bass.ds(e + (3 * P - 1), 1)], min_val=0, max_val=MAX_ITEMS)
                for q in range(CHUNKS):
                    if q < 8:
                        sp_.wait_ge(gu_made, done * KT + (2 * (q // 2) + 2))
                    else:
                        sp_.wait_ge(dn_made, done * 4 + (q - 8 + 1))
                    sp_.dma_start(chunk_tile(q), chunk_source(e, q)).then_inc(w_arrived[q], SEMW)

            total = item_count(sp_)
            sp_.wait_ge(gu_made, total * KT)
            sp_.dma_start(final_g, ins["final_g"].rearrange("(a n) -> a n", a=1).broadcast_to([P, D])
                          ).then_inc(fing_in, SEMW)
            sp_.wait_ge(acc_out, total * (HALVES * SEMW) + SEMW * TT)
            for t in range(TT):
                sp_.dma_start(h_rows[:, t, :], acc_rows[t * P:(t + 1) * P, :]).then_inc(fin_in[t], SEMW)
            for t in range(TT):
                sp_.wait_ge(fin_made, t + 1)
                sp_.dma_start(out_rows[t * P:(t + 1) * P, :], h_rows[:, t, :]).then_inc(stored, SEMW)
            sp_.wait_ge(stored, SEMW * TT)

        @block.gpsimd
        def _(pool):
            chain = [0]

            def link(ins_):
                chain[0] += 1
                ins_.then_inc(pool_chain, 1)
                pool.wait_ge(pool_chain, chain[0])

            link(pool.memset(ident[:, :], 0.0))
            link(pool.affine_select(out=ident[:, :], in_=ident[:, :], compare_op=ALU.not_equal, fill=1.0, base=0,
                                    pattern=[[-1, P]], channel_multiplier=1))
            link(pool.memset(ones[:, :], 1.0))
            link(pool.memset(before[:, :], 1.0))
            link(pool.affine_select(out=before[:, :], in_=before[:, :], compare_op=ALU.is_gt, fill=0.0, base=0,
                                    pattern=[[1, P]], channel_multiplier=-1))
            link(pool.memset(eps[:, :], EPS))
            link(pool.memset(tiny[:, :], 1e-30))
            link(pool.memset(s5[:, 2560:3584], 0.0))
            link(pool.iota(iota_s[:, :], pattern=[[1, SLOTS]], base=0, channel_multiplier=0,
                           allow_small_or_imprecise_dtypes=True))
            link(pool.iota(iota_e[:, :], pattern=[[1, NE]], base=0, channel_multiplier=0,
                           allow_small_or_imprecise_dtypes=True))
            link(pool.iota(pidx[:, :], pattern=[[0, 1]], base=0, channel_multiplier=1,
                           allow_small_or_imprecise_dtypes=True))
            link(pool.iota(tokpart[:, :, 0], pattern=[[1, TT]], base=-TT, channel_multiplier=0,
                           allow_small_or_imprecise_dtypes=True))
            link(pool.iota(tokpart[:, :, 1], pattern=[[0, TT]], base=0, channel_multiplier=1,
                           allow_small_or_imprecise_dtypes=True))
            link(pool.memset(tokpart[:, :, 2], 1.0))
            link(pool.iota(slot_c[:, 0, :], pattern=[[P, HALVES]], base=S, channel_multiplier=1,
                           allow_small_or_imprecise_dtypes=True))
            link(pool.iota(slot_c[:, 1, :], pattern=[[-P, HALVES]], base=0, channel_multiplier=-1,
                           allow_small_or_imprecise_dtypes=True))
            pool.memset(big[:, 4, 0:D], 0.0).then_inc(const_made, 1)

            pool.wait_ge(const_made, 1)
            zero = big[:, 4, 0:D]
            pool.dma_start(hs_rows[S:S + P, :], zero).then_inc(hs_out, SEMW)
            pool.dma_start(hs_rows[S + P:S + 2 * P, :], zero).then_inc(hs_out, SEMW)
            pool.dma_start(acc_rows[S:S + P, :], zero).then_inc(hs_out, SEMW)
            pool.dma_start(acc_rows[S + P:S + 2 * P, :], zero).then_inc(hs_out, SEMW)
            pool.dma_start(wm_raw, ins["sgu_w"][0].rearrange("h t s -> t h s")).then_inc(wm_in, SEMW)
            for s in range(2):
                for bd, w in ((wr_bd, "lru_wr"), (wi_bd, "lru_wi")):
                    pool.dma_start(bd[64 * s:64 * s + 64, :, 64 * s:64 * s + 64],
                                   ins[w][0].rearrange("(c s) i o -> s i c o", s=2)[s]).then_inc(mixpar_in, SEMW)
                pool.dma_start(sgu_bias[64 * s:64 * s + 64, :, :],
                               ins["sgu_b"].rearrange("a (h s) t -> s a h t", s=2)[s].broadcast_to([64, 4, P])
                               ).then_inc(mixpar_in, SEMW)
            for dst, src in ((ln_g, "sgu_ln_g"), (ln_b, "sgu_ln_b")):
                pool.dma_start(dst, ins[src].broadcast_to([P, DL])).then_inc(mixpar_in, SEMW)
            pool.dma_start(router_w, ins["router_w"][0].rearrange("(k p) e -> p k e", p=P)).then_inc(mixpar_in, SEMW)
            pool.dma_start(rbias[:, :], ins["router_b"].rearrange("a e -> e a")).then_inc(mixpar_in, SEMW)

            pool.wait_ge(rstd_made, 1)
            for t in range(TT):
                pool.tensor_scalar(x_rows[:, t, :], x_rows[:, t, :], rstd[:, t:t + 1], None, ALU.mult
                                   ).then_inc(x_scaled, 1)
            pool.wait_ge(dve_drained, drained_by(JOB[("wm", 1)])[1])
            pool.affine_select(out=wmT, in_=wmT, compare_op=ALU.is_ge, fill=0.0, base=0,
                               pattern=[[0, 8], [1, P]], channel_multiplier=-1).then_inc(wm_masked, 1)
            pool.wait_ge(mixpar_in, SEMW * 10)
            for t in range(TT):
                pool.wait_ge(v_normed, t + 1)
                link(pool.tensor_tensor(v_rows[:, t, :], v_rows[:, t, :], ln_g, ALU.mult))
                pool.tensor_tensor(v_rows[:, t, :], v_rows[:, t, :], ln_b, ALU.add).then_inc(v_affine, 1)
            for t in range(TT):
                pool.wait_ge(hs_made, t + 1)
                pool.dma_start(hs_rows[t * P:(t + 1) * P, :], hs_tile[:, t % 4, :]).then_inc(hs_out, SEMW)
            pool.wait_ge(filled, JOB[("wo", (TT - 1, 1))] + 1)
            pool.dma_start(bgu_raw, ins["exp_b_gu"][0]).then_inc(bgu_in, SEMW)
            pool.dma_start(bdown_raw, ins["exp_b_down"][0]).then_inc(bgu_in, SEMW)
            pool.wait_ge(hs_out, SEMW * (4 + TT))
            for t in range(TT):
                pool.wait_ge(acc_made, t + 1)
                pool.dma_start(acc_rows[t * P:(t + 1) * P, :], h_rows[:, t, :]).then_inc(acc_out, SEMW)
            def gather(turn):
                pool.wait_ge(idx_made, turn + 1)
                pool.sem_inc(may_start, 1)
                for h in range(HALVES):
                    pool.indirect_dma_start(zg[:, h, :], None, hs_rows,
                                            bass.IndirectOffsetOnAxis(ap=idx_next[:, h:h + 1], axis=0)
                                            ).then_inc(rows_in[h], SEMW)

            pool.wait_ge(items_ready, 1)
            gather(0)
            total = item_count(pool)
            base = chain[0]
            with pool.Fori(0, total) as g:
                for f in range(KT):
                    if f == 3:
                        pool.wait_ge(zt_made, g * 4 + 4)
                        gather(g + 1)
                    pool.wait_ge(sig_made, g * KT + (f + 1))
                    if f >= 2:
                        pool.wait_ge(act_made, g * KT + (f - 1))
                    pool.tensor_tensor(glu_t[:, 3, f % 2, :], glu_t[:, 0, f % 2, :], glu_t[:, 2, f % 2, :], ALU.mult
                                       ).then_inc(gsig_made, 1)
                pool.wait_ge(yt_drained, g * 4 + 5)
                pool.wait_ge(acc_out, g * (HALVES * SEMW) + SEMW * TT)
                pool.sem_inc(may_start, 1)
                for h in range(HALVES):
                    pool.indirect_dma_start(acc_rows, bass.IndirectOffsetOnAxis(ap=idx_cur[:, h:h + 1], axis=0),
                                            y_rows[:, h, :], None, bounds_check=S + TRASH - 1, compute_op=ALU.add
                                            ).then_inc(acc_out, SEMW)
            pool.wait_ge(rows_in[0], (total + 1) * SEMW)
            pool.wait_ge(rows_in[1], (total + 1) * SEMW)

        @block.scalar
        def _(act):
            chain = [0]

            def link(ins_):
                chain[0] += 1
                ins_.then_inc(act_chain, 1)
                act.wait_ge(act_chain, chain[0])

            def take(name, i):
                n = JOB[(name, i)]
                act.wait_ge(filled, n + 1)
                return bank_of(n)

            act.wait_ge(const_made, 1)
            act.wait_ge(dve_drained, 1)
            act.activation(cact[:, :], cols[:, ROW["c"]:ROW["c"] + 8], ACT.Silu).then_inc(cact_made, 1)
            for t in range(TT):
                act.wait_ge(x_in[t], SEMW)
                link(act.activation(r1[:, 0:D], x_rows[:, t, :], ACT.Square, accum_out=ssum[:, t:t + 1]))
            act.activation(srt[:, :], ssum[:, :], ACT.Sqrt, bias=eps[:, 0:1], scale=1.0 / D).then_inc(sqrt_made, 1)
            act.wait_ge(sp_exp, 1)
            act.activation(sp[:, 2, :], sp[:, 1, :], ACT.Exp, scale=-1.0).then_inc(sp_exp, 1)
            act.wait_ge(affine_made, 1)
            for th in range(2):
                for k in range(KT):
                    b = take("zT", (k, th))
                    act.activation(zT[:, k, th * 512:(th + 1) * 512], b, ACT.Identity, bias=mod[:, SH1 + k:SH1 + k + 1],
                                   scale=scale1[:, k:k + 1]).then_inc(act_drained, 1)
            for ct in range(CT):
                for th in range(2):
                    b = take("ya", (ct, th))
                    act.activation(yaT[:, ct, th * 512:(th + 1) * 512], b, ACT.Gelu_apprx_tanh).then_inc(act_drained, 1)
                if ct == 0:
                    act.wait_ge(sp_made, 1)
                if ct > 0:
                    act.wait_ge(lru_made, ct)
                for g, bias, i in (("rec", "lru_br", 1), ("inp", "lru_bi", 2)):
                    for th in range(2):
                        b = take(g, (ct, th))
                        ins_ = act.activation(lru_t[:, i, th * 512:(th + 1) * 512], b, ACT.Sigmoid,
                                              bias=cols[:, ROW[bias] + ct:ROW[bias] + ct + 1])
                        ins_.then_inc(act_drained, 1)
                act.wait_ge(act_drained, drained_by(JOB[("inp", (ct, 1))])[1])
                link(act.activation(lru_t[:, 3, :], lru_t[:, 1, :], ACT.Exp, scale=sp[:, 7, ct:ct + 1]))
                act.activation(lru_t[:, 1, :], lru_t[:, 1, :], ACT.Tanh, scale=sp[:, 6, ct:ct + 1]).then_inc(decay_made, 1)
                act.wait_ge(mult2_made, ct + 1)
                act.activation(lru_t[:, 0, :], lru_t[:, 0, :], ACT.Sqrt, bias=tiny[:, 0:1]).then_inc(mult_made, 1)
            for m in range(CT):
                for th in range(2):
                    b = take("u", (m, th))
                    act.activation(uT[:, m, th * 512:(th + 1) * 512], b, ACT.Gelu_apprx_tanh).then_inc(act_drained, 1)
            for t in range(TT):
                b = take("v", t)
                act.activation(v_rows[:, t, :], b, ACT.Gelu_apprx_tanh).then_inc(act_drained, 1)
            act.wait_ge(bn_made, 1)
            act.activation(srt[:, :], bn2[:, :, 1], ACT.Sqrt, bias=eps[:, 0:1]).then_inc(bn_root, 1)
            for grp, src in ((0, yaT), (1, uT)):
                act.wait_ge(sgu_made if grp else lru_made, TT if grp else CT)
                for ct in range(CT):
                    act.activation(lru_t[:, ct, :], src[:, ct, :], ACT.Square).then_inc(squares, 1)
                for th in range(2):
                    b = take("ssq", (grp, th))
                    act.activation(xaT[:, 2 * grp + th, 0:512], b, ACT.Sqrt, bias=eps[:, 0:1], scale=1.0 / DL
                                   ).then_inc(act_drained, 1)
            for th in range(2):
                for t in range(4 * th, 4 * th + 4):
                    act.wait_ge(dve_drained, drained_by(JOB[("wo", (t, 1))])[1])
                    if t == 0:
                        act.wait_ge(heads_made, 2 * CT)
                    if t == 4:
                        act.wait_ge(hs_out, SEMW * (4 + 4))
                        act.wait_ge(filled, JOB[("z2T", (KT - 1, 0))] + 1)
                    link(act.activation(hs_tile[:, t % 4, :], h_rows[:, t, :], ACT.Square, accum_out=ssum[:, t:t + 1]))
                act.activation(srt[:, 4 * th:4 * th + 4], ssum[:, 4 * th:4 * th + 4], ACT.Sqrt, bias=eps[:, 0:1],
                               scale=1.0 / D).then_inc(h_root, 1)
                act.wait_ge(h_rstd, th + 1)
                for t in range(4 * th, 4 * th + 4):
                    act.activation(hs_tile[:, t % 4, :], h_rows[:, t, :], ACT.Copy, scale=rstd[:, t:t + 1]
                                   ).then_inc(hs_made, 1)
                for k in range(KT):
                    b = take("z2T", (k, th))
                    if th == 1 and k == 0:
                        act.wait_ge(filled, JOB[("lgT", 0)] + 1)
                    act.activation(z2T[:, k, :], b, ACT.Identity, bias=mod[:, SH2 + k:SH2 + k + 1],
                                   scale=scale2[:, k:k + 1]).then_inc(act_drained, 1)
                b = take("lgT", th)
                if th == 0:
                    act.wait_ge(mixpar_in, SEMW * 10)
                act.activation(lgT_sb[:, th * 512:(th + 1) * 512], b[0:NE, :], ACT.Identity, bias=rbias[:, 0:1]
                               ).then_inc(act_drained, 1)
            act.wait_ge(top_made, 1)
            act.activation(ex4, ex4, ACT.Exp).then_inc(exp_made, 1)
            act.activation(gate, gate, ACT.Exp).then_inc(exp_made, 1)

            def transposed_rows(turn):
                for kk in range(4):
                    act.wait_ge(zt_made, turn * 4 + (kk + 1))
                    for i in range(2):
                        k = 2 * kk + i
                        ins_ = act.activation(izT[:, k, :], psum[:, 2 + kk % 2, i * SLOTS:(i + 1) * SLOTS], ACT.Identity,
                                              bias=mod[:, SH2 + k:SH2 + k + 1], scale=scale2[:, k:k + 1])
                    ins_.then_inc(zt_drained, 1)

            act.wait_ge(items_ready, 1)
            transposed_rows(0)
            total = item_count(act)
            with act.Fori(0, total) as g:
                for f in range(KT):
                    act.wait_ge(gu_drained, g * KT + (f + 1))
                    if f >= 2:
                        act.wait_ge(gsig_made, g * KT + (f - 1))
                    act.activation(glu_t[:, 2, f % 2, :], glu_t[:, 0, f % 2, :], ACT.Sigmoid, scale=ALPHA
                                   ).then_inc(sig_made, 1)
                transposed_rows(g + 1)
                for pr in range(4):
                    act.wait_ge(dn_made, g * 4 + (pr + 1))
                    if pr >= 2:
                        act.wait_ge(yt_made, g * 4 + (pr - 1))
                    for i in range(2):
                        k = 2 * pr + i
                        ins_ = act.activation(yT[:, pr % 2, i, :], psum[:, 4 + pr % 2, i * SLOTS:(i + 1) * SLOTS],
                                              ACT.Copy, scale=mod[:, G2 + k:G2 + k + 1])
                    ins_.then_inc(dn_drained, 1)
            for t in range(TT):
                act.wait_ge(fin_in[t], SEMW)
                act.activation(r2[:, t * D:(t + 1) * D], h_rows[:, t, :], ACT.Square, accum_out=ssum[:, t:t + 1]
                               ).then_inc(fin_sum, 1)
                act.wait_ge(fin_sum, t + 1)
                act.activation(srt[:, t:t + 1], ssum[:, t:t + 1], ACT.Sqrt, bias=eps[:, 0:1], scale=1.0 / D
                               ).then_inc(fin_root, 1)

        @block.tensor
        def _(pe):
            def open_bank(name, i):
                n = JOB[(name, i)]
                if n >= BANKS:
                    wait_drained(pe, n - BANKS)
                return bank_of(n)

            def dense_ready(key):
                n = DENSE_AT[key]
                pe.wait_ge(dense_in[n % DENSE_SLOTS], SEMW * (n // DENSE_SLOTS + 1))

            def mod_cols(j):
                b = open_bank("mod", j)
                pe.wait_ge(gemv_made, j + 1)
                for i in range(4):
                    last = pe.matmul(b[:, i:i + 1], gacc[:, j % 2, i * P:(i + 1) * P], ones[:, 0:1],
                                     start=(i == 0), stop=True, skip_group_check=True)
                last.then_inc(filled, 1)

            def gate_row(name, q, turn):
                b = open_bank(name, q)
                pe.wait_ge(diag_made, turn + 1)
                pe.matmul(b, ones[:, :], gacc[:, q, :], start=True, stop=True).then_inc(filled, 1)

            def project(name, key, m, th):
                b = open_bank(name, (m, th))
                w = ring(key)
                for k in range(KT):
                    last = pe.matmul(b, w[:, k, m * P:(m + 1) * P], zT[:, k, th * 512:(th + 1) * 512],
                                     start=(k == 0), stop=(k == KT - 1))
                last.then_inc(filled, 1)

            pe.wait_ge(param_in, SEMW * len(PARAM_ROWS))
            pe.wait_ge(const_made, 1)
            b = open_bank("cols", 0)
            pe.transpose(b[:, 0:NROWS], prow[0:NROWS, :], ident[0:NROWS, 0:NROWS]).then_inc(filled, 1)
            for j in range(4):
                mod_cols(j)
            for th in range(2):
                pe.wait_ge(x_scaled, 4 * th + 4)
                for k in range(KT):
                    b = open_bank("zT", (k, th))
                    for i in range(4):
                        last = pe.transpose(b[:, i * P:(i + 1) * P], x_rows[:, 4 * th + i, k * P:(k + 1) * P], ident[:, :])
                    last.then_inc(filled, 1)
            dense_ready(("win", 0))
            pe.wait_ge(act_drained, drained_by(JOB[("zT", (KT - 1, 1))])[1])
            for m in range(CT):
                for th in range(2):
                    project("xa", ("win", 0), m, th)
            for j in (4, 5):
                mod_cols(j)
            for q in range(2):
                gate_row("g1row", q, q)
            dense_ready(("win", 1))
            pe.wait_ge(mixpar_in, SEMW * 10)
            for ct in range(CT):
                for th in range(2):
                    project("ya", ("win", 1), ct, th)
                pe.wait_ge(conv_made, ct + 1)
                for name, w in (("rec", wr_bd), ("inp", wi_bd)):
                    for th in range(2):
                        b = open_bank(name, (ct, th))
                        pe.matmul(b, w[:, ct, :], lru_t[:, 0, th * 512:(th + 1) * 512], start=True, stop=True
                                  ).then_inc(filled, 1)
                if ct >= 2:
                    mod_cols(4 + ct)
            pe.wait_ge(wm_in, SEMW)
            for q in range(2):
                b = open_bank("wm", q)
                for i in range(4):
                    last = pe.transpose(b[:, i * P:(i + 1) * P], wm_raw[:, 4 * q + i, :], ident[:, :])
                last.then_inc(filled, 1)
            dense_ready(("win", 2))
            for m in range(CT):
                for th in range(2):
                    project("u", ("win", 2), m, th)
            for j in (8, 9):
                mod_cols(j)
            dense_ready(("win", 3))
            for t in range(TT):
                b = open_bank("v", t)
                for k in range(KT):
                    last = pe.matmul(b, zT[:, k, t * P:(t + 1) * P], ring(("win", 3))[:, k, :],
                                     start=(k == 0), stop=(k == KT - 1))
                last.then_inc(filled, 1)
            for j in (10, 11):
                mod_cols(j)
            for q in range(2):
                gate_row("g2row", q, 2 + q)

            def sum_squares(grp):
                pe.wait_ge(squares, CT * (grp + 1))
                for th in range(2):
                    b = open_bank("ssq", (grp, th))
                    for ct in range(CT):
                        last = pe.matmul(b, ones[:, :], lru_t[:, ct, th * 512:(th + 1) * 512],
                                         start=(ct == 0), stop=(ct == CT - 1))
                    last.then_inc(filled, 1)

            sum_squares(0)
            pe.wait_ge(wm_masked, 1)
            for t in range(TT):
                pe.wait_ge(v_affine, t + 1)
                b = open_bank("mix", t)
                for hp in range(4):
                    for s in range(2):
                        h = 2 * hp + s
                        last = pe.matmul(b[64 * s:64 * s + 64, hp * P:(hp + 1) * P], v_rows[:, t, h * 64:(h + 1) * 64],
                                         wmT[:, h, :], start=(hp == 0), stop=True, skip_group_check=True)
                last.then_inc(filled, 1)
            sum_squares(1)
            for th in range(2):
                for t in range(4 * th, 4 * th + 4):
                    for dh in range(2):
                        if t == 0:
                            pe.wait_ge(wout_scaled, dh + 1)
                            pe.wait_ge(heads_made, 2 * CT)
                        b = open_bank("wo", (t, dh))
                        for ct in range(2 * CT):
                            src = yaT if ct < CT else uT
                            last = pe.matmul(b, src[:, ct % CT, t * P:(t + 1) * P], ring(("wout", dh))[:, ct, :],
                                             start=(ct == 0), stop=(ct == 2 * CT - 1))
                        last.then_inc(filled, 1)
            for th in range(2):
                pe.wait_ge(hs_made, 4 * th + 4)
                for k in range(KT):
                    b = open_bank("z2T", (k, th))
                    for i in range(4):
                        last = pe.transpose(b[:, i * P:(i + 1) * P], hs_tile[:, i, k * P:(k + 1) * P], ident[:, :])
                    last.then_inc(filled, 1)
                b = open_bank("lgT", th)
                for k in range(KT):
                    pe.wait_ge(act_drained, drained_by(JOB[("z2T", (k, th))])[1])
                    last = pe.matmul(b[0:NE, :], router_w[:, k, :], z2T[:, k, :], start=(k == 0), stop=(k == KT - 1))
                last.then_inc(filled, 1)
            b = open_bank("lg", 0)
            pe.wait_ge(act_drained, drained_by(JOB[("lgT", 1)])[1])
            for t in range(TT):
                last = pe.transpose(b[:, t * NE:(t + 1) * NE], lgT_sb[:, t * P:(t + 1) * P], ident[0:NE, 0:NE])
            last.then_inc(filled, 1)
            b = open_bank("bgu", 0)
            pe.wait_ge(bgu_in, SEMW * 2)
            for f in range(16):
                last = pe.transpose(b[:, f * NE:(f + 1) * NE], bgu_raw[:, f * P:(f + 1) * P], ident[0:NE, 0:NE])
            last.then_inc(filled, 1)
            pe.wait_ge(sel_made, 1)
            for i, w in ((0, before), (1, ones)):
                b = open_bank("rank", i)
                pe.matmul(b[:, 0:TT * NE], w[:, :], sel.rearrange("p t e -> p (t e)"), start=True, stop=True
                          ).then_inc(filled, 1)
            b = open_bank("items", 0)
            pe.wait_ge(item_f_made, 1)
            for i in range(3):
                last = pe.matmul(b[0:1, i * P:(i + 1) * P], it_c[:, i:i + 1], ident[:, :], start=(i == 0), stop=True,
                                 skip_group_check=True)
            last.then_inc(filled, 1)
            for q in range(2):
                b = open_bank("gT", q)
                for i in range(4):
                    last = pe.transpose(b[0:NE, i * P:(i + 1) * P], gate[:, 4 * q + i, :], ident[:, :])
                last.then_inc(filled, 1)
            pe.wait_ge(dve_drained, drained_by(JOB[("gT", 1)])[1])
            for t in range(TT):
                for dh in range(2):
                    b = open_bank("bd", (t, dh))
                    pe.matmul(b, gT[:, t * P:(t + 1) * P], bdown_raw[:, dh * 512:(dh + 1) * 512], start=True, stop=True
                              ).then_inc(filled, 1)
            pe.wait_ge(act_drained, LAST_ACT)
            pe.wait_ge(dve_drained, LAST_DVE)

            def make_list(turn):
                pe.wait_ge(hot_made, turn + 1)
                if not (isinstance(turn, int) and turn == 0):
                    pe.wait_ge(list_read, turn)
                for h in range(HALVES):
                    for t in range(TT):
                        last = pe.matmul(psum[:, 6, h * 8:h * 8 + 6], onehot[:, t, h * P:(h + 1) * P], cur6[:, t, :],
                                         start=(t == 0), stop=(t == TT - 1), skip_group_check=True)
                last.then_inc(list_made, 1)

            def transpose_rows(turn):
                for h in range(HALVES):
                    pe.wait_ge(rows_in[h], (turn + 1) * SEMW)
                for kk in range(4):
                    if kk >= 2:
                        pe.wait_ge(zt_drained, turn * 4 + (kk - 1))
                    for i in range(2):
                        for h in range(HALVES):
                            last = pe.transpose(psum[:, 2 + kk % 2, i * SLOTS + h * P:i * SLOTS + (h + 1) * P],
                                                zg[:, h, (2 * kk + i) * P:(2 * kk + i + 1) * P], ident[:, :])
                    last.then_inc(zt_made, 1)

            def transpose_results(g, pr):
                pe.wait_ge(dn_drained, g * 4 + (pr + 1))
                pe.wait_ge(yt_drained, g * 4 + (pr + 1))
                for h in range(HALVES):
                    for i in range(2):
                        last = pe.transpose(psum[:, 7, h * SLOTS + i * P:h * SLOTS + (i + 1) * P],
                                            yT[:, pr % 2, i, h * P:(h + 1) * P], ident[:, :])
                last.then_inc(yt_made, 1)

            pe.wait_ge(items_ready, 1)
            make_list(0)
            transpose_rows(0)
            make_list(1)
            total = item_count(pe)
            with pe.Fori(0, total) as g:
                e = item_value(pe, 0, g, 0, NE - 1)
                rest = item_value(pe, 2, g, 0, S)
                arrived = pe.snap(e * SEMW + SEMW)

                def gate_and_linear(width):
                    for f in range(KT):
                        if f % 2 == 0:
                            pe.wait_ge(w_arrived[f], arrived)
                            pe.wait_ge(w_arrived[f + 1], arrived)
                        if f >= 2:
                            pe.wait_ge(gu_drained, g * KT + (f - 1))
                        for part in range(2):
                            w = chunk_tile(2 * (f // 2) + part)
                            for k in range(KT):
                                last = pe.matmul(psum[:, f % 2, part * SLOTS:part * SLOTS + width],
                                                 w[:, k, (f % 2) * P:(f % 2 + 1) * P], izT[:, k, 0:width],
                                                 start=(k == 0), stop=(k == KT - 1))
                        last.then_inc(gu_made, 1)

                def down(width):
                    for pr in range(4):
                        pe.wait_ge(w_arrived[8 + pr], arrived)
                        if pr >= 2:
                            pe.wait_ge(dn_drained, g * 4 + (pr - 1))
                        w = chunk_tile(8 + pr)
                        for i in range(2):
                            for f in range(KT):
                                if pr == 0 and i == 0:
                                    pe.wait_ge(act_made, g * KT + (f + 1))
                                last = pe.matmul(psum[:, 4 + pr % 2, i * SLOTS:i * SLOTS + width],
                                                 w[:, f, i * P:(i + 1) * P], actT[:, f, 0:width],
                                                 start=(f == 0), stop=(f == KT - 1))
                        last.then_inc(dn_made, 1)
                        if pr > 0:
                            transpose_results(g, pr - 1)

                def by_width(body, widths):
                    if len(widths) == 1:
                        body(widths[0])
                        return
                    mid = len(widths) // 2
                    with pe.If(rest < widths[mid - 1] + 1):
                        by_width(body, widths[:mid])
                        pe.nop()
                    with pe.Else():
                        by_width(body, widths[mid:])
                        pe.nop()

                pe.wait_ge(zt_drained, g * 4 + 4)
                by_width(gate_and_linear, WIDTHS)
                transpose_rows(g + 1)
                by_width(down, WIDTHS)
                make_list(g + 2)
                transpose_results(g, 3)

        @block.vector
        def _(dve):
            chain = [0]

            def link(ins_):
                chain[0] += 1
                ins_.then_inc(dve_chain, 1)
                dve.wait_ge(dve_chain, chain[0])

            def take(name, i):
                n = JOB[(name, i)]
                dve.wait_ge(filled, n + 1)
                return bank_of(n)

            def col(name, i=0, n=1):
                return cols[:, ROW[name] + i:ROW[name] + i + n]

            b = take("cols", 0)
            dve.tensor_copy(cols[:, :], b[:, 0:NROWS]).then_inc(dve_drained, 1)
            dve.wait_ge(dve_drained, 1)
            link(dve.tensor_scalar(sp[:, 0, :], col("lru_lambda", 0, 4), -1.0, None, ALU.mult))
            dve.tensor_tensor(sp[:, 1, :], col("lru_lambda", 0, 4), sp[:, 0, :], ALU.max).then_inc(sp_exp, 1)

            def mod_products(j):
                n = DENSE_AT[("ada", j)]
                dve.wait_ge(dense_in[n % DENSE_SLOTS], SEMW * (n // DENSE_SLOTS + 1))
                if j >= 2:
                    dve.wait_ge(filled, JOB[("mod", j - 2)] + 1)
                w, a = ring(("ada", j)), gacc[:, j % 2, :]
                link(dve.tensor_scalar(a, w[:, 0, :], cact[:, 0:1], None, ALU.mult))
                for k in range(1, KT):
                    ins_ = dve.scalar_tensor_tensor(out=a, in0=w[:, k, :], scalar=cact[:, k:k + 1], in1=a,
                                                    op0=ALU.mult, op1=ALU.add)
                    if k < KT - 1:
                        link(ins_)
                ins_.then_inc(gemv_made, 1)

            def mod_add(j):
                b = take("mod", j)
                dve.tensor_tensor(mod[:, 4 * j:4 * j + 4], b[:, 0:4], col("ada_b", 4 * j, 4), ALU.add
                                  ).then_inc(dve_drained, 1)

            dve.wait_ge(cact_made, 1)
            mod_products(0)
            mod_products(1)
            mod_add(0)
            mod_products(2)
            dve.wait_ge(sqrt_made, 1)
            dve.reciprocal(rstd[:, :], srt[:, :]).then_inc(rstd_made, 1)
            mod_add(1)
            mod_products(3)
            mod_add(2)
            mod_add(3)
            dve.wait_ge(dve_drained, drained_by(JOB[("mod", 3)])[1])
            link(dve.tensor_scalar(scale1[:, :], mod[:, SC1:SC1 + 8], 1.0, None, ALU.add))
            dve.tensor_tensor(scale1[:, :], scale1[:, :], col("norm1_g", 0, 8), ALU.mult).then_inc(affine_made, 1)
            dve.wait_ge(sp_exp, 2)
            link(dve.tensor_scalar(sp[:, 3, :], sp[:, 2, :], 2.0, None, ALU.add))
            link(dve.reciprocal(sp[:, 3, :], sp[:, 3, :]))
            link(dve.tensor_tensor(sp[:, 3, :], sp[:, 3, :], sp[:, 2, :], ALU.mult))
            link(dve.tensor_tensor(sp[:, 4, :], sp[:, 3, :], sp[:, 3, :], ALU.mult))
            link(dve.tensor_scalar(sp[:, 5, :], sp[:, 4, :], 1.0 / 17, None, ALU.mult))
            for d in (15, 13, 11, 9, 7, 5, 3):
                link(dve.scalar_tensor_tensor(out=sp[:, 5, :], in0=sp[:, 5, :], scalar=1.0 / d, in1=sp[:, 4, :],
                                              op0=ALU.add, op1=ALU.mult))
            link(dve.scalar_tensor_tensor(out=sp[:, 5, :], in0=sp[:, 5, :], scalar=1.0, in1=sp[:, 3, :],
                                          op0=ALU.add, op1=ALU.mult))
            link(dve.tensor_scalar(sp[:, 0, :], sp[:, 0, :], 0.0, None, ALU.max))
            link(dve.scalar_tensor_tensor(out=sp[:, 5, :], in0=sp[:, 5, :], scalar=2.0, in1=sp[:, 0, :],
                                          op0=ALU.mult, op1=ALU.add))
            link(dve.tensor_scalar(sp[:, 6, :], sp[:, 5, :], 8.0, None, ALU.mult))
            dve.tensor_scalar(sp[:, 7, :], sp[:, 5, :], -8.0, None, ALU.mult).then_inc(sp_made, 1)

            def conv(ct):
                w = [col("conv_w", 4 * j + ct) for j in range(4)]
                link(dve.tensor_scalar(lru_t[:, 0, :], xaT[:, ct, :], w[3], col("conv_b", ct), ALU.mult, ALU.add))
                for j in (1, 2, 3):
                    ins_ = dve.scalar_tensor_tensor(out=lru_t[:, 0, j:S], in0=xaT[:, ct, 0:S - j], scalar=w[3 - j],
                                                    in1=lru_t[:, 0, j:S], op0=ALU.mult, op1=ALU.add)
                    if j < 3:
                        link(ins_)
                ins_.then_inc(conv_made, 1)

            def recurrence(ct):
                dve.wait_ge(act_drained, drained_by(JOB[("inp", (ct, 1))])[1])
                link(dve.tensor_tensor(lru_t[:, 2, :], lru_t[:, 2, :], lru_t[:, 0, :], ALU.mult))
                dve.wait_ge(decay_made, ct + 1)
                link(dve.tensor_tensor(lru_t[:, 0, :], lru_t[:, 3, :], lru_t[:, 3, :], ALU.mult))
                dve.scalar_tensor_tensor(out=lru_t[:, 0, :], in0=lru_t[:, 0, :], scalar=1.0, in1=lru_t[:, 1, :],
                                         op0=ALU.add, op1=ALU.mult).then_inc(mult2_made, 1)
                dve.wait_ge(mult_made, ct + 1)
                link(dve.tensor_tensor(lru_t[:, 2, :], lru_t[:, 2, :], lru_t[:, 0, :], ALU.mult))
                link(dve.tensor_tensor_scan(lru_t[:, 0, :], lru_t[:, 3, :], lru_t[:, 2, :], 0.0, ALU.mult, ALU.add))
                dve.tensor_tensor(yaT[:, ct, :], yaT[:, ct, :], lru_t[:, 0, :], ALU.mult).then_inc(lru_made, 1)
                dve.wait_ge(lru_made, ct + 1)

            for m in range(CT):
                for th in range(2):
                    b = take("xa", (m, th))
                    dve.tensor_copy(xaT[:, m, th * 512:(th + 1) * 512], b).then_inc(dve_drained, 1)
                if m == 0:
                    dve.wait_ge(dve_drained, drained_by(JOB[("xa", (0, 1))])[1])
                    dve.wait_ge(hs_out, SEMW * 4)
                    conv(0)
                if m < 2:
                    mod_products(4 + m)
            dve.wait_ge(dve_drained, drained_by(JOB[("xa", (CT - 1, 1))])[1])

            def gate_rows(name, first, dst, turn):
                for q in range(2):
                    for i in range(4):
                        k = first + 4 * q + i
                        ins_ = dve.tensor_scalar(gacc[:, q, i * P:(i + 1) * P], ident[:, :], mod[:, k:k + 1], None, ALU.mult)
                        if i < 3:
                            link(ins_)
                    ins_.then_inc(diag_made, 1)
                for q in range(2):
                    b = take(name, q)
                    dve.tensor_copy(dst[:, q * 512:(q + 1) * 512], b).then_inc(dve_drained, 1)

            mod_add(4)
            mod_add(5)
            dve.wait_ge(dve_drained, drained_by(JOB[("mod", 5)])[1])
            gate_rows("g1row", G1, g1row, 0)
            for ct in range(CT):
                recurrence(ct)
                if ct + 1 < CT:
                    conv(ct + 1)
                if ct == 0:
                    mod_products(6)
                if ct == 2:
                    mod_products(7)
            mod_add(6)
            mod_add(7)
            for q in range(2):
                b = take("wm", q)
                dve.tensor_copy(wmT[:, 4 * q:4 * q + 4, :], b.rearrange("p (h t) -> p h t", h=4)).then_inc(dve_drained, 1)
            for j in (8, 9):
                mod_products(j)
            for j in (8, 9):
                mod_add(j)
            for j in (10, 11):
                mod_products(j)
            for t in range(TT):
                dve.wait_ge(act_drained, drained_by(JOB[("v", t)])[1])
                link(dve.bn_stats(bn6[:, :], v_rows[:, t, :]))
                ins_ = dve.bn_aggr(bn2[:, t, :], bn6[:, :])
                if t < TT - 1:
                    link(ins_)
            ins_.then_inc(bn_made, 1)
            dve.wait_ge(bn_root, 1)
            link(dve.reciprocal(rstd[:, :], srt[:, :]))
            for t in range(TT):
                dve.tensor_scalar(v_rows[:, t, :], v_rows[:, t, :], bn2[:, t, 0:1], rstd[:, t:t + 1],
                                  ALU.subtract, ALU.mult).then_inc(v_normed, 1)
            mod_add(10)
            mod_add(11)
            dve.wait_ge(dve_drained, drained_by(JOB[("mod", 11)])[1])
            link(dve.tensor_scalar(scale2[:, :], mod[:, SC2:SC2 + 8], 1.0, None, ALU.add))
            link(dve.tensor_tensor(scale2[:, :], scale2[:, :], col("norm2_g", 0, 8), ALU.mult))
            gate_rows("g2row", G2, g2row, 2)

            def norm_heads(grp, src, gain):
                dve.wait_ge(act_drained, drained_by(JOB[("ssq", (grp, 1))])[1])
                for th in range(2):
                    link(dve.reciprocal(xaT[:, 2 * grp + th, 512:1024], xaT[:, 2 * grp + th, 0:512]))
                for ct in range(CT):
                    for th in range(2):
                        ins_ = dve.scalar_tensor_tensor(
                            out=src[:, ct, th * 512:(th + 1) * 512], in0=src[:, ct, th * 512:(th + 1) * 512],
                            scalar=col(gain, ct), in1=xaT[:, 2 * grp + th, 512:1024], op0=ALU.mult, op1=ALU.mult)
                    ins_.then_inc(heads_made, 1)

            norm_heads(0, yaT, "gnorm_lru_g")
            dve.wait_ge(mixpar_in, SEMW * 10)
            dve.wait_ge(act_drained, drained_by(JOB[("v", TT - 1)])[1])
            for t in range(TT):
                b = take("mix", t)
                tmp = gacc[:, t % 2, :].rearrange("p (h t) -> p h t", h=4)
                dve.tensor_tensor(tmp, b.rearrange("p (h t) -> p h t", h=4), sgu_bias, ALU.add).then_inc(dve_drained, 1)
                dve.wait_ge(dve_drained, drained_by(JOB[("mix", t)])[1])
                u = uT[:, :, t * P:(t + 1) * P]
                dve.tensor_tensor(u, u, tmp, ALU.mult).then_inc(sgu_made, 1)
            dve.wait_ge(dve_drained, drained_by(JOB[("g1row", 1)])[1])
            for dh in range(2):
                n = DENSE_AT[("wout", dh)]
                dve.wait_ge(dense_in[n % DENSE_SLOTS], SEMW * (n // DENSE_SLOTS + 1))
                w = ring(("wout", dh))
                g = g1row[:, dh * 512:(dh + 1) * 512].unsqueeze(1).broadcast_to([P, 8, 512])
                dve.tensor_tensor(w, w, g, ALU.mult).then_inc(wout_scaled, 1)
            dve.wait_ge(sgu_made, TT)
            norm_heads(1, uT, "gnorm_sgu_g")
            for th in range(2):
                for t in range(4 * th, 4 * th + 4):
                    dve.wait_ge(xr_in[t], SEMW)
                    for dh in range(2):
                        b = take("wo", (t, dh))
                        hh = h_rows[:, t, dh * 512:(dh + 1) * 512]
                        dve.tensor_tensor(hh, b, hh, ALU.add).then_inc(dve_drained, 1)
                dve.wait_ge(h_root, th + 1)
                dve.reciprocal(rstd[:, 4 * th:4 * th + 4], srt[:, 4 * th:4 * th + 4]).then_inc(h_rstd, 1)

            b = take("lg", 0)
            link(dve.memset(lg36[:, :, NE:NE + 4], NEG))
            dve.tensor_copy(lg36[:, :, 0:NE], b[:, 0:TT * NE].rearrange("p (t e) -> p t e", t=TT)).then_inc(dve_drained, 1)
            dve.wait_ge(dve_drained, drained_by(JOB[("lg", 0)])[1])
            for t in range(TT):
                link(dve.max(out=top8[:, t, :], in_=lg36[:, t, 0:NE]))
            link(dve.tensor_tensor(ex4, top8[:, :, 0:TOPK], top8[:, :, 0:1].broadcast_to([P, TT, TOPK]), ALU.subtract))
            dve.tensor_tensor(gate, lg36[:, :, 0:NE], top8[:, :, 0:1].broadcast_to([P, TT, NE]), ALU.subtract
                              ).then_inc(top_made, 1)
            dve.wait_ge(top_made, 1)
            link(dve.memset(top8[:, :, TOPK:8], NEG))
            for t in range(TT):
                link(dve.match_replace(out=mr36[:, t, :], in_to_replace=top8[:, t, :], in_values=lg36[:, t, :],
                                       imm_value=3.0e38))
            dve.tensor_tensor(sel, mr36[:, :, 0:NE], lg36[:, :, 0:NE], ALU.not_equal).then_inc(sel_made, 1)
            dve.wait_ge(sel_made, 1)
            b = take("bgu", 0)
            bb = b.rearrange("p (f e) -> p f e", f=16)
            link(dve.tensor_copy(bgu_col[:, 0:8, :], bb[:, 0:8, :]))
            dve.tensor_scalar(bgu_col[:, 8:16, :], bb[:, 8:16, :], 1.0, None, ALU.add).then_inc(dve_drained, 1)
            dve.wait_ge(exp_made, 2)
            link(dve.tensor_reduce(rsum, ex4, AX.X, ALU.add))
            link(dve.reciprocal(rsum, rsum))
            link(dve.tensor_tensor(gate, gate, sel, ALU.mult))
            link(dve.tensor_tensor(gate, gate, rsum.unsqueeze(2).broadcast_to([P, TT, NE]), ALU.mult))
            link(dve.tensor_copy(gate_tab[:, :, :, 3], gate.rearrange("p t e -> p e t")))
            link(dve.tensor_tensor(gtmp, gate, gate_tab[:, :, :, 3].rearrange("p e t -> p t e"), ALU.subtract))
            link(dve.tensor_copy(gate_tab[:, :, :, 4], gtmp.rearrange("p t e -> p e t")))
            link(dve.tensor_tensor(gtmp, gtmp, gate_tab[:, :, :, 4].rearrange("p e t -> p t e"), ALU.subtract))
            link(dve.tensor_copy(gate_tab[:, :, :, 5], gtmp.rearrange("p t e -> p e t")))
            for i in range(3):
                link(dve.tensor_copy(gate_tab[:, :, :, i], tokpart[:, :, i].unsqueeze(1).broadcast_to([P, NE, TT])))
            b = take("rank", 0)
            dve.tensor_copy(rank, b[:, 0:TT * NE].rearrange("p (t e) -> p t e", t=TT)).then_inc(dve_drained, 1)
            dve.wait_ge(dve_drained, drained_by(JOB[("rank", 0)])[1])
            b = take("rank", 1)
            link(dve.memset(run_off[:, :], 0.0))
            for t in range(TT):
                link(dve.tensor_tensor(rank[:, t, :], rank[:, t, :], run_off[:, :], ALU.add))
                ins_ = dve.tensor_tensor(run_off[:, :], run_off[:, :], b[:, t * NE:(t + 1) * NE], ALU.add)
                if t < TT - 1:
                    link(ins_)
            ins_.then_inc(dve_drained, 1)
            dve.wait_ge(dve_drained, drained_by(JOB[("rank", 1)])[1])
            link(dve.scalar_tensor_tensor(out=rank, in0=rank, scalar=1.0, in1=sel, op0=ALU.add, op1=ALU.mult))
            for i in range(NB):
                link(dve.tensor_scalar(rank_at[:, i, :, :], rank.rearrange("p t e -> p e t"), -1.0 - SLOTS * i, None, ALU.add))
            count, nitem, cum, mask, tmp, zero_e = (it_f[:, i, :] for i in range(6))
            link(dve.tensor_copy(count, run_off[:, :]))
            link(dve.memset(zero_e, 0.0))
            link(dve.tensor_scalar(nitem, count, float(SLOTS), 1.0, ALU.is_gt, ALU.add))
            for i in range(2, NB):
                link(dve.scalar_tensor_tensor(out=nitem, in0=count, scalar=float(SLOTS * i), in1=nitem,
                                              op0=ALU.is_gt, op1=ALU.add))
            link(dve.tensor_tensor_scan(cum, nitem, zero_e, 0.0, ALU.add, ALU.add))
            link(dve.tensor_scalar(mask, cum, pidx[:, 0:1], None, ALU.is_le))
            link(dve.tensor_reduce(it_c[:, 3:4], mask, AX.X, ALU.add))
            link(dve.tensor_scalar(it_c[:, 0:1], it_c[:, 3:4], float(NE - 1), None, ALU.min))
            link(dve.tensor_tensor(tmp, mask, nitem, ALU.mult))
            link(dve.tensor_reduce(it_c[:, 4:5], tmp, AX.X, ALU.add))
            link(dve.tensor_tensor(it_c[:, 4:5], pidx[:, 0:1], it_c[:, 4:5], ALU.subtract))
            link(dve.tensor_scalar(it_c[:, 4:5], it_c[:, 4:5], float(NB - 1), 0.0, ALU.min, ALU.max))
            link(dve.tensor_scalar(mask, iota_e[:, :], it_c[:, 0:1], None, ALU.is_equal))
            link(dve.tensor_tensor(tmp, mask, count, ALU.mult))
            link(dve.tensor_reduce(it_c[:, 5:6], tmp, AX.X, ALU.add))
            link(dve.scalar_tensor_tensor(out=it_c[:, 2:3], in0=it_c[:, 4:5], scalar=-float(SLOTS), in1=it_c[:, 5:6],
                                          op0=ALU.mult, op1=ALU.add))
            dve.scalar_tensor_tensor(out=it_c[:, 1:2], in0=it_c[:, 4:5], scalar=float(NE), in1=it_c[:, 0:1],
                                     op0=ALU.mult, op1=ALU.add).then_inc(item_f_made, 1)
            b = take("items", 0)
            link(dve.tensor_scalar(items_i[0:1, 3 * P:3 * P + NE], cum[0:1, :], -1.0, None, ALU.add))
            link(dve.tensor_copy(items_i[0:1, 3 * P + NE:3 * P + NE + 1], cum[0:1, NE - 1:NE]))
            dve.tensor_copy(items_i[0:1, 0:3 * P], b[0:1, 0:3 * P]).then_inc(dve_drained, 1)
            dve.wait_ge(dve_drained, drained_by(JOB[("items", 0)])[1])
            dve.sem_inc(items_ready, 1)

            for q in range(2):
                b = take("gT", q)
                dve.tensor_copy(gT[:, q * 512:(q + 1) * 512], b[0:NE, :]).then_inc(dve_drained, 1)
            for t in range(TT):
                for dh in range(2):
                    b = take("bd", (t, dh))
                    tmp2 = gacc[:, dh, :]
                    dve.tensor_tensor(tmp2, b, g2row[:, dh * 512:(dh + 1) * 512], ALU.mult).then_inc(dve_drained, 1)
                    dve.wait_ge(dve_drained, drained_by(JOB[("bd", (t, dh))])[1])
                    hh = h_rows[:, t, dh * 512:(dh + 1) * 512]
                    link(dve.tensor_tensor(hh, hh, tmp2, ALU.add))
                dve.sem_inc(acc_made, 1)

            def make_onehot(turn):
                at = item_value(dve, 1, turn, 0, NB * NE - 1)
                e = item_value(dve, 0, turn, 0, NE - 1)
                ranks = rank_at.rearrange("p b e t -> p (b e t)")[:, bass.ds(at * TT, TT)]
                dve.tensor_copy(cur6[:, :, :], gate_tab.rearrange("p e t i -> p (e t i)")[:, bass.ds(e * (TT * 6), TT * 6)]
                                .rearrange("p (t i) -> p t i", t=TT))
                dve.tensor_tensor(onehot, iota_s[:, :].unsqueeze(1).broadcast_to([P, TT, SLOTS]),
                                  ranks.unsqueeze(2).broadcast_to([P, TT, SLOTS]), ALU.is_equal).then_inc(hot_made, 1)

            def read_list(turn, step):
                dve.wait_ge(list_made, turn + 1)
                step(dve.tensor_copy(lst[:, :, :], psum[:, 6, 0:HALVES * 8].rearrange("p (h i) -> p h i", h=HALVES)[:, :, 0:6]))
                dve.sem_inc(list_read, 1)
                step(dve.scalar_tensor_tensor(out=lst_t[:, 0, :], in0=lst[:, :, 0], scalar=float(P), in1=slot_c[:, 0, :],
                                              op0=ALU.mult, op1=ALU.add))
                step(dve.tensor_tensor(lst_t[:, 1, :], lst[:, :, 2], slot_c[:, 1, :], ALU.mult))
                step(dve.tensor_tensor(lst_t[:, 0, :], lst_t[:, 0, :], lst[:, :, 1], ALU.add))
                step(dve.tensor_tensor(lst_t[:, 2, :], lst[:, :, 4], lst[:, :, 5], ALU.add))
                step(dve.tensor_tensor(gate_next[:, :], lst[:, :, 3], lst_t[:, 2, :], ALU.add))
                dve.tensor_tensor(idx_next[:, :], lst_t[:, 0, :], lst_t[:, 1, :], ALU.add).then_inc(idx_made, 1)

            def activate(g, f):
                dve.wait_ge(gsig_made, g * KT + (f + 1))
                dve.scalar_tensor_tensor(out=actT[:, f, :], in0=glu_t[:, 1, f % 2, :], scalar=1.0 - LIMIT,
                                         in1=glu_t[:, 3, f % 2, :], op0=ALU.max, op1=ALU.mult).then_inc(act_made, 1)

            READ_STEPS = 6
            dve.sem_inc(yt_drained, 1)
            make_onehot(0)
            read_list(0, link)
            make_onehot(1)
            dve.wait_ge(idx_made, 1)
            total = item_count(dve)
            base = chain[0]
            STEPS = 3 + READ_STEPS
            with dve.Fori(0, total) as g:
                count_ = [0]

                def step(ins_):
                    count_[0] += 1
                    ins_.then_inc(dve_chain, 1)
                    dve.wait_ge(dve_chain, g * STEPS + (base + count_[0]))

                e = item_value(dve, 0, g, 0, NE - 1)
                step(dve.tensor_copy(bg_cur[:, :], bgu_col.rearrange("p f e -> p (f e)")[:, bass.DynSlice(e, 16, step=NE)]))
                for f in range(KT):
                    dve.wait_ge(gu_made, g * KT + (f + 1))
                    if f >= 2:
                        dve.wait_ge(act_made, g * KT + (f - 1))
                    dve.tensor_scalar(glu_t[:, 1, f % 2, :], psum[:, f % 2, SLOTS:2 * SLOTS], bg_cur[:, 8 + f:9 + f],
                                      LIMIT + 1.0, ALU.add, ALU.min)
                    dve.tensor_scalar(glu_t[:, 0, f % 2, :], psum[:, f % 2, 0:SLOTS], bg_cur[:, f:f + 1],
                                      LIMIT, ALU.add, ALU.min).then_inc(gu_drained, 1)
                    if f == 2:
                        dve.wait_ge(acc_out, g * (HALVES * SEMW) + SEMW * TT)
                        step(dve.tensor_copy(idx_cur[:, :], idx_next[:, :]))
                        step(dve.tensor_copy(gate_cur[:, :], gate_next[:, :]))
                        dve.wait_ge(rows_in[0], (g + 1) * SEMW)
                        dve.wait_ge(rows_in[1], (g + 1) * SEMW)
                        read_list(g + 1, step)
                    if f >= 1:
                        activate(g, f - 1)
                activate(g, KT - 1)
                make_onehot(g + 2)
                for pr in range(4):
                    dve.wait_ge(yt_made, g * 4 + (pr + 1))
                    for h in range(HALVES):
                        ins_ = dve.tensor_scalar(y_rows[:, h, pr * 256:(pr + 1) * 256],
                                                 psum[:, 7, h * SLOTS:(h + 1) * SLOTS],
                                                 gate_cur[:, h:h + 1], None, ALU.mult)
                    ins_.then_inc(yt_drained, 1)
                assert count_[0] == STEPS
            dve.wait_ge(fing_in, SEMW)
            for t in range(TT):
                dve.wait_ge(fin_root, t + 1)
                dve.reciprocal(rstd[:, t:t + 1], srt[:, t:t + 1]).then_inc(fin_rstd, 1)
                dve.wait_ge(fin_rstd, t + 1)
                dve.scalar_tensor_tensor(out=h_rows[:, t, :], in0=h_rows[:, t, :], scalar=rstd[:, t:t + 1],
                                         in1=final_g, op0=ALU.mult, op1=ALU.mult).then_inc(fin_made, 1)


_INS = ['x', 'c', 'ada_w', 'ada_b', 'norm1_g', 'w_in', 'conv_w', 'conv_b', 'lru_wr', 'lru_br', 'lru_wi', 'lru_bi',
        'lru_lambda', 'sgu_ln_g', 'sgu_ln_b', 'sgu_w', 'sgu_b', 'gnorm_lru_g', 'gnorm_sgu_g', 'w_out', 'norm2_g',
        'router_w', 'router_b', 'exp_w_gu', 'exp_b_gu', 'exp_w_down', 'exp_b_down', 'final_g']


def kernel(**inputs):
    import numpy as _np
    import concourse.bacc as _bacc
    from concourse import mybir as _mybir
    from concourse.bass_utils import run_bass_kernel_spmd as _run

    nc = _bacc.Bacc("TRN2", target_bir_lowering=False, num_devices=1)
    arrays, ins = {}, {}
    for name in _INS:
        a = _np.ascontiguousarray(inputs[name])
        arrays[f"in_{name}_dram"] = a
        ins[name] = nc.dram_tensor(f"in_{name}_dram", a.shape, _mybir.dt.from_np(a.dtype), kind="ExternalInput").ap()
    out = nc.dram_tensor("out_dram", (1, S, D), _mybir.dt.float32, kind="ExternalOutput").ap()
    build(nc, ins, out)
    r = _run(nc, [arrays], core_ids=[0])
    return r.results[0]["out_dram"]
```
